# Optimizing a Trainium2 kernel written in Bass

```python
import jax, jax.numpy as jnp
from jax import lax
import numpy as np

D_MODEL = 1024
BATCH = 1
SEQ = 512
DEPTH = 1
DEC_BATCH = 8
DEC_SEQ = 16
PAST_LEN = 128

CHUNK = 64
D_CONV = D_MODEL
CONV_W = 3
RET_HEADS = 4
RET_DK = D_MODEL // RET_HEADS
RET_DV = D_MODEL // RET_HEADS
D_RET_V = RET_HEADS * RET_DV
D_MIX = D_MODEL
ROPE_BASE = 10000.0
PEER_HEADS = 8
N_KEYS = 128
N_EXPERTS = N_KEYS * N_KEYS
PEER_TOPK = 16
D_KEY = 256
D_HALF = D_KEY // 2
PEER_BLOCK = 128
EPS = 1e-6
IN_SPLITS = (D_CONV, D_CONV, D_CONV, RET_HEADS * RET_DK, RET_HEADS * RET_DK, D_RET_V, D_RET_V, D_MIX, D_MIX)
D_IN = 3 * D_CONV + 2 * RET_HEADS * RET_DK + 2 * D_RET_V + 2 * D_MIX

kernel_name = 'hybrid_conv_retention_peer_stream_step'

def _rmsnorm(x, g):
    xf = x.astype(jnp.float32)
    y = xf * lax.rsqrt(jnp.mean(xf * xf, axis=-1, keepdims=True) + EPS)
    return (y * g.astype(jnp.float32)).astype(x.dtype)

def _ret_log_decay():
    return jnp.log1p(-jnp.exp2(-5.0 - jnp.arange(RET_HEADS, dtype=jnp.float32)))

def _rope(x, pos):
    half = x.shape[-1] // 2
    inv = ROPE_BASE ** (-jnp.arange(half, dtype=jnp.float32) / half)
    ang = pos.astype(jnp.float32)[:, None] * inv[None, :]
    cos = jnp.cos(ang)[None, :, None, :]
    sin = jnp.sin(ang)[None, :, None, :]
    x1 = x[..., :half].astype(jnp.float32)
    x2 = x[..., half:].astype(jnp.float32)
    return jnp.concatenate([x1 * cos - x2 * sin, x1 * sin + x2 * cos], axis=-1)

def _ret_chunk(S, qkv):
    q, k, v = qkv
    L = q.shape[2]
    lg = _ret_log_decay()
    n = jnp.arange(L, dtype=jnp.float32)
    diff = n[:, None] - n[None, :]
    decay = jnp.where(diff >= 0, jnp.exp(lg[:, None, None] * jnp.maximum(diff, 0.0)), 0.0)
    att = jnp.einsum('bhld,bhmd->bhlm', q, k) * decay
    o = (jnp.einsum('bhlm,bhme->bhle', att, v)
         + jnp.einsum('bhld,bhde->bhle', q, S) * jnp.exp(lg[:, None] * (n + 1.0))[:, :, None])
    kw = k * jnp.exp(lg[:, None] * (L - 1.0 - n))[:, :, None]
    S_new = jnp.exp(lg * L)[:, None, None] * S + jnp.einsum('bhmd,bhme->bhde', kw, v)
    return S_new, o

def _retention(q, k, v, S0):
    b, h, L, _ = q.shape
    if L <= CHUNK:
        return _ret_chunk(S0, (q, k, v))
    nc = L // CHUNK

    def split(t):
        return jnp.moveaxis(t.reshape(b, h, nc, CHUNK, t.shape[-1]), 2, 0)

    S, o = lax.scan(_ret_chunk, S0, (split(q), split(k), split(v)))
    o = jnp.moveaxis(o, 0, 2).reshape(b, h, L, v.shape[-1])
    return S, o

def _mixer(h, conv_state, ret_state, pos, w_in, conv_w, w_out):
    b, l, _ = h.shape
    pts = np.cumsum(IN_SPLITS)[:-1].tolist()
    cb, cc, ch, q, k, v, rg, ga, gb = jnp.split(h @ w_in, pts, axis=-1)
    u = cc * ch
    ext = jnp.concatenate([conv_state.astype(u.dtype), u], axis=1)
    conv = ext[:, 0:l] * conv_w[0] + ext[:, 1:l + 1] * conv_w[1] + ext[:, 2:l + 2] * conv_w[2]
    y_conv = cb * conv
    new_conv = ext[:, -(CONV_W - 1):]
    qh = jnp.transpose(_rope(q.reshape(b, l, RET_HEADS, RET_DK), pos), (0, 2, 1, 3))
    kh = jnp.transpose(_rope(k.reshape(b, l, RET_HEADS, RET_DK), pos) * (RET_DK ** -0.5), (0, 2, 1, 3))
    vh = jnp.transpose(v.reshape(b, l, RET_HEADS, RET_DV).astype(jnp.float32), (0, 2, 1, 3))
    S, o = _retention(qh, kh, vh, ret_state.astype(jnp.float32))
    o = o * lax.rsqrt(jnp.mean(o * o, axis=-1, keepdims=True) + EPS)
    o = jnp.transpose(o, (0, 2, 1, 3)).reshape(b, l, D_RET_V).astype(h.dtype)
    y_ret = jax.nn.silu(rg) * o
    m = jax.nn.sigmoid(ga) * y_conv + jax.nn.sigmoid(gb) * y_ret
    return m @ w_out, new_conv, S.astype(ret_state.dtype)

def _peer(h, w_q, sub_keys, u_tab, v_tab):
    b, l, d = h.shape
    T = b * l
    pad = (-T) % PEER_BLOCK
    blocks = jnp.pad(h.reshape(T, d), ((0, pad), (0, 0))).reshape(-1, PEER_BLOCK, d)
    sk = sub_keys.astype(jnp.float32)

    def blk(hb):
        q = (hb @ w_q).reshape(PEER_BLOCK, PEER_HEADS, 2, D_HALF).astype(jnp.float32)
        s = jnp.einsum('thpd,pkd->thpk', q, sk)
        sv, si = lax.top_k(s, PEER_TOPK)
        cand = (sv[:, :, 0, :, None] + sv[:, :, 1, None, :]).reshape(PEER_BLOCK, PEER_HEADS, PEER_TOPK * PEER_TOPK)
        cidx = (si[:, :, 0, :, None] * N_KEYS + si[:, :, 1, None, :]).reshape(PEER_BLOCK, PEER_HEADS, PEER_TOPK * PEER_TOPK)
        ts, tp = lax.top_k(cand, PEER_TOPK)
        e = jnp.take_along_axis(cidx, tp, axis=-1)
        g = jax.nn.softmax(ts, axis=-1)
        a = jax.nn.gelu(jnp.einsum('thkd,td->thk', u_tab[e], hb).astype(jnp.float32), approximate=False)
        return jnp.einsum('thk,thkd->td', (g * a).astype(hb.dtype), v_tab[e])

    out = lax.map(blk, blocks).reshape(-1, d)[:T]
    return out.reshape(b, l, d)

def _layer(x, conv_state, ret_state, pos, norm1, w_in, conv_w, w_out, norm2, wq, sk, u_tab, v_tab):
    m, cs, rs = _mixer(_rmsnorm(x, norm1), conv_state, ret_state, pos, w_in, conv_w, w_out)
    x = x + m
    x = x + _peer(_rmsnorm(x, norm2), wq, sk, u_tab, v_tab)
    return x, cs, rs

def setup_inputs(seed: int = 0) -> dict:
    key = jax.random.key(seed)
    ks = jax.random.split(key, 15)
    nrm = jax.random.normal
    f32 = jnp.float32
    return {
        'x_prompt': nrm(ks[0], (BATCH, SEQ, D_MODEL), f32),
        'x_sample': nrm(ks[1], (DEC_BATCH, DEC_SEQ, D_MODEL), f32),
        'state_conv': nrm(ks[2], (DEPTH, DEC_BATCH, CONV_W - 1, D_CONV), f32),
        'state_ret': nrm(ks[3], (DEPTH, DEC_BATCH, RET_HEADS, RET_DK, RET_DV), f32) * RET_DK ** -0.5,
        'norm1_g': 1.0 + 0.02 * nrm(ks[4], (DEPTH, D_MODEL), f32),
        'w_in': nrm(ks[5], (DEPTH, D_MODEL, D_IN), f32) * D_MODEL ** -0.5,
        'conv_w': nrm(ks[6], (DEPTH, CONV_W, D_CONV), f32) * CONV_W ** -0.5,
        'w_out': nrm(ks[7], (DEPTH, D_MIX, D_MODEL), f32) * D_MIX ** -0.5,
        'norm2_g': 1.0 + 0.02 * nrm(ks[8], (DEPTH, D_MODEL), f32),
        'peer_wq': nrm(ks[9], (DEPTH, D_MODEL, PEER_HEADS * D_KEY), f32) * D_MODEL ** -0.5,
        'peer_subkeys': nrm(ks[10], (DEPTH, 2, N_KEYS, D_HALF), f32) * D_HALF ** -0.5,
        'peer_u': nrm(ks[11], (DEPTH, N_EXPERTS, D_MODEL), f32) * D_MODEL ** -0.5,
        'peer_v': nrm(ks[12], (DEPTH, N_EXPERTS, D_MODEL), f32) * PEER_HEADS ** -0.5,
        'final_g': 1.0 + 0.02 * nrm(ks[13], (D_MODEL,), f32),
    }

def reference(x_prompt, x_sample, state_conv, state_ret, norm1_g, w_in, conv_w, w_out, norm2_g,
              peer_wq, peer_subkeys, peer_u, peer_v, final_g):
    bp, lp, _ = x_prompt.shape
    ls = x_sample.shape[1]
    pos_p = jnp.arange(lp)
    pos_s = PAST_LEN + jnp.arange(ls)
    zero_conv = jnp.zeros((bp, CONV_W - 1, D_CONV), x_prompt.dtype)
    zero_ret = jnp.zeros((bp, RET_HEADS, RET_DK, RET_DV), x_prompt.dtype)
    xp, xs = x_prompt, x_sample
    cp_l, rp_l, cs_l, rs_l = [], [], [], []
    for i in range(DEPTH):
        ws = (norm1_g[i], w_in[i], conv_w[i], w_out[i], norm2_g[i], peer_wq[i], peer_subkeys[i], peer_u[i], peer_v[i])
        xp, cp, rp = _layer(xp, zero_conv, zero_ret, pos_p, *ws)
        xs, cs, rs = _layer(xs, state_conv[i], state_ret[i], pos_s, *ws)
        cp_l.append(cp)
        rp_l.append(rp)
        cs_l.append(cs)
        rs_l.append(rs)
    y_prompt = _rmsnorm(xp, final_g)
    y_sample = _rmsnorm(xs, final_g)
    new_conv_prompt = jnp.stack(cp_l)
    new_ret_prompt = jnp.stack(rp_l)
    new_conv_sample = jnp.stack(cs_l)
    new_ret_sample = jnp.stack(rs_l)
    return (y_prompt, y_sample, new_conv_prompt, new_ret_prompt, new_conv_sample, new_ret_sample)


_drawn_inputs = setup_inputs


def setup_inputs(seed=0):
    import zlib

    import numpy as np

    out = dict(_drawn_inputs(seed))
    spreads = {}
    factors = {}
    for name, (base, spread) in spreads.items():
        noise = np.random.default_rng([zlib.crc32(name.encode()), seed]).standard_normal(out[name].shape)
        drawn = base * np.exp(spread * noise) if base else spread * noise
        out[name] = __import__('jax').numpy.asarray(drawn.astype(out[name].dtype))
    for name, factor in factors.items():
        out[name] = (out[name] * factor).astype(out[name].dtype)
    return out
```

```python
from contextlib import ExitStack

import numpy as np

import concourse.bass as bass
from concourse import mybir
from concourse.alu_op_type import AluOpType as ALU

F32 = mybir.dt.float32
F32R = mybir.dt.float32r
BF16 = mybir.dt.bfloat16
U32 = mybir.dt.uint32
ACT = mybir.ActivationFunctionType
AX = mybir.AxisListType
ds = bass.ds

P = 128
D = 1024
KT = D // P
PROMPT, STREAMS, STEP = 512, 8, 16
T = PROMPT + STREAMS * STEP
TT = T // P
PT = PROMPT // P
HALF = T // 2
PAST = 128
CONV_W = 3
HEADS, DK, DV = 4, 256, 256
PH, NKEY, TOPK = 8, 128, 16
SIDES = 2 * PH
GROUP = 4
NE_GROUPS = NKEY // GROUP
EPS = 1e-6
SPLITS = {n: i * KT for i, n in enumerate(("cb", "cc", "ch", "q", "k", "v", "rg", "ga", "gb"))}
A_MIX = 9 * KT
N_WOUT = KT
A_WQ = SIDES
UB = 2 + PROMPT + STREAMS * (STEP + 2)
CW = UB - 2
BLK = 8
GT = 64
LOWEST = -3.0e38


def w_in_order():
    order = []
    for h in range(HEADS):
        for name in ("q", "k", "v", "rg"):
            order += [SPLITS[name] + 2 * h, SPLITS[name] + 2 * h + 1]
    order += [SPLITS["gb"] + c for c in range(KT)]
    for c in range(KT):
        order += [SPLITS[name] + c for name in ("cc", "ch", "cb", "ga")]
    return order


def tables():
    f = np.float32
    half = DK // 2
    pos = np.concatenate([np.arange(PROMPT), np.tile(PAST + np.arange(STEP), STREAMS)]).astype(f)
    inv = np.power(f(10000.0), -np.arange(half, dtype=f) / f(half)).astype(f)
    ang = (pos[None, :] * inv[:, None]).astype(f)
    lg = np.log1p(-np.exp2(-5.0 - np.arange(HEADS)))
    x, m = np.arange(PROMPT)[None, :], np.arange(P)[:, None]
    scale = DK ** -0.5
    dec = np.stack([np.where(x >= m, np.exp(g * np.maximum(x - m, 0)), 0.0) * scale for g in lg], 1)
    l = np.arange(P)[None, :]
    same = (l // STEP == m // STEP) & (l >= m)
    dec_s = np.stack([np.where(same, np.exp(g * np.maximum(l - m, 0)), 0.0) * scale for g in lg], 1)
    gq = np.stack([np.broadcast_to(np.exp(g * (l % STEP + 1)), (P, P)) for g in lg], 1)
    kcol = np.zeros((P, HEADS, PT + STREAMS))
    for h, g in enumerate(lg):
        for j in range(PT):
            kcol[:, h, j] = np.exp(g * (PROMPT - 1 - j * P - np.arange(P))) * scale
        for b in range(STREAMS):
            r = np.arange(P)
            kcol[:, h, PT + b] = np.where(r // STEP == b, np.exp(g * (STEP - 1 - r % STEP)), 0.0) * scale
    g16 = np.broadcast_to(np.exp(lg * STEP)[None, :], (P, HEADS))
    parts = {
        "cos": np.cos(ang), "sin": np.sin(ang), "dec": dec.reshape(P, -1), "dec_s": dec_s.reshape(P, -1),
        "gq": gq.reshape(P, -1), "kcol": kcol.reshape(P, -1), "g16": g16,
        "ident": np.eye(P), "ones": np.full((P, P), 1.0 / DV),
        "iota16": np.broadcast_to(np.arange(TOPK)[None, :], (P, TOPK)),
    }
    return {k: np.ascontiguousarray(v, dtype=f) for k, v in parts.items()}


class Line:

    def __init__(self, eng, sem):
        self.eng, self.sem, self.base, self.n = eng, sem, 0, 0

    def turn(self, i, per):
        self.start, self.per = self.base + self.n, per
        self.base, self.n = self.start + i * per, 0

    def close(self, turns):
        assert self.n == self.per, (self.n, self.per)
        self.base, self.n = self.start + turns * self.per, 0

    def mark(self, ins):
        ins.then_inc(self.sem, 1)
        self.n += 1

    def then(self, ins):
        self.mark(ins)
        self.eng.wait_ge(self.sem, self.base + self.n)


def build_program(nc, io):
    ctx = ExitStack()
    with ctx:
        names = [0]

        def at(off, shape, dt):
            names[0] += 1
            return nc.alloc_sbuf_tensor_at(f"b{names[0]}", shape, dt, offset=off)

        def take(cursor, shape, dt):
            n = int(np.prod(shape[1:])) * (2 if dt == BF16 else 4)
            n = (n + 31) // 32 * 32
            t = at(cursor[0], shape, dt)
            cursor[0] += n
            assert cursor[0] <= nc.sbuf_usable_end, cursor[0]
            return t

        def sem(name):
            return ctx.enter_context(nc.semaphore(name))

        base = [(nc.sbuf_base + 63) // 64 * 64]
        h_hi = take(base, [P, KT, T], F32R)
        h_lo = take(base, [P, KT, T], F32R)
        x = take(base, [P, TT, D], F32)
        raw = take(base, [P, GROUP, D], F32)
        wa_hi = [take(base, [P, D], F32R) for _ in range(GROUP)]
        wa_lo = [take(base, [P, D], F32R) for _ in range(GROUP)]
        ident = take(base, [P, P], F32)
        ones = take(base, [P, P], F32)
        g1 = take(base, [P, KT], F32)
        g2 = take(base, [P, KT], F32)
        ss = take(base, [P, TT], F32)
        rms = take(base, [P, TT], F32)
        rstd = take(base, [P, TT], F32)
        vs = take(base, [P, TT], F32)
        eps = take(base, [P, 1], F32)
        nothing = take(base, [P, 1], F32)
        after = base[0]

        r = [after]
        yret = take(r, [P, KT, T], F32)
        conv_from = r[0]
        qk_raw = take(r, [P, 4, T], F32)
        qT = take(r, [P, 2, T], F32)
        kT = take(r, [P, 2, T], F32)
        vT = take(r, [P, 2, T], F32)
        cos = take(r, [P, T], F32)
        sin = take(r, [P, T], F32)
        dec = take(r, [P, HEADS, PROMPT], F32)
        dec_s = take(r, [P, HEADS, P], F32)
        gq = take(r, [P, HEADS, P], F32)
        kcol = take(r, [P, HEADS, PT + STREAMS], F32)
        g16 = take(r, [P, HEADS], F32)
        kv = take(r, [P, TT, DK + DV], F32)
        kw = take(r, [P, 4, DK], F32)
        att = take(r, [P, 1408], F32)
        s_in = take(r, [P, 4, 2, DV], F32)
        s_out = take(r, [P, 2, 2, DV], F32)
        att_at = [0, 512, 896, 1152, 1280]
        att_n = [512, 384, 256, 128, 128]
        o_sb = qk_raw
        xs = at(conv_from, [P, 2, D], F32)
        hf = at(conv_from + 8192, [P, 2, 512], F32)

        c = [conv_from]
        m_hi = take(c, [P, KT, T], F32R)
        m_lo = take(c, [P, KT, T], F32R)
        newc = take(c, [P, KT, 2 + 2 * STREAMS], F32)
        c_in = take(c, [P, 4, T], F32)
        gate = take(c, [P, 2, T], F32)
        ub = take(c, [P, UB], F32)
        cv = take(c, [P, UB], F32)
        y = take(c, [P, T], F32)
        convw = take(c, [P, KT, CONV_W], F32)
        sconv = take(c, [P, KT, 2 * STREAMS], F32)

        top = nc.sbuf_usable_end // 64 * 64
        wb = [top - 8 * D * 4]
        wb_hi = [take(wb, [P, D], F32R) for _ in range(GROUP)]
        wb_lo = [take(wb, [P, D], F32R) for _ in range(GROUP)]

        k = [after]
        k1T = take(k, [P, T], BF16)
        k2T = take(k, [P, T], BF16)
        w3T = take(k, [P, 3, T], BF16)
        one_from = k[0]
        qpT = take(k, [P, SIDES, T], F32)
        skT = take(k, [P, 2, NKEY], F32)
        q_cur = take(k, [P, SIDES, P], F32)
        rest = take(k, [P, SIDES, NKEY], F32)
        val = take(k, [P, SIDES, TOPK], F32)
        idx = take(k, [P, SIDES, TOPK], U32)
        idx_f = take(k, [P, SIDES, TOPK], F32)
        cand = take(k, [P, PH, TOPK * TOPK], F32)
        cand2 = take(k, [P, PH, TOPK * TOPK], F32)
        ts = take(k, [P, PH, TOPK], F32)
        tp = take(k, [P, PH, TOPK], U32)
        tij = take(k, [P, 2, PH * TOPK], U32)
        tij_f = take(k, [P, 2, PH * TOPK], F32)
        iota16 = take(k, [P, TOPK], F32)
        pick = take(k, [P, 3, PH * TOPK], F32)
        mx = take(k, [P, 3, PH], F32)
        wT = take(k, [P, P], F32)
        wT2 = take(k, [P, P], F32)
        xs2 = at(one_from, [P, 2, D], F32)
        hf2 = at(one_from + 8192, [P, 2, 512], F32)

        o = [one_from]
        iotaK = take(o, [P, NKEY, BLK], BF16)
        eq1 = take(o, [P, 2, NKEY, BLK], BF16)
        eq2 = take(o, [P, 2, NKEY, BLK], BF16)
        ew = take(o, [P, 2, 3, NKEY, BLK], BF16)
        gts = [take(o, [P, NKEY, GT], F32) for _ in range(2)]

        e = [after]
        p_hi = [take(e, [P, GROUP, T], F32R) for _ in range(2)]
        p_lo = [take(e, [P, GROUP, T], F32R) for _ in range(2)]
        gl = take(e, [P, 2, T], F32)
        gr = take(e, [P, GROUP, T], F32)
        p32 = take(e, [P, T], F32)
        assert e[0] <= top - 8 * D * 4
        fin_g = at(after, [P, D], F32)
        fin_y = at(after + D * 4, [P, 2, D], F32)

        ps = ctx.enter_context(nc.psum_tensor("ps", [P, 8, 512], F32))
        gates = nc.dram_tensor("gates", [P, NKEY, T], F32).ap()

        loaded = [sem(f"raw_loaded{u}") for u in range(GROUP)]
        hi_ready = sem("hi_ready")
        lo_ready = sem("lo_ready")
        a_used = sem("a_used")
        evac = sem("evac")
        consts = sem("norm_consts_loaded")
        ret_consts = sem("retention_consts_loaded")
        conv_consts = sem("conv_consts_loaded")
        peer_consts = sem("retrieval_consts_loaded")
        x_loaded = sem("x_loaded")
        xs_ready = sem("xs_ready")
        xsT_done = sem("xsT_done")
        h_ready = sem("h_ready")
        eps_ready = sem("eps_ready")
        dve_chain = sem("dve_chain")
        act_chain = sem("act_chain")
        qk_ready = sem("qk_ready")
        kvT_done = sem("kvT_done")
        kv_ready = sem("kv_ready")
        att_done = sem("att_done")
        att_ready = sem("att_ready")
        kw_ready = sem("kw_ready")
        o_done = sem("o_done")
        o_ready = sem("o_ready")
        st_done = sem("st_done")
        st_ready = sem("st_ready")
        st_stored = [sem(f"st_stored{i}") for i in range(2)]
        s_loaded = [sem(f"s_loaded{i}") for i in range(4)]
        qg_ready = sem("qg_ready")
        cross_done = sem("cross_done")
        sq_ready = sem("sq_ready")
        ms_done = sem("ms_done")
        orms_ready = sem("orms_ready")
        yret_ready = sem("yret_ready")
        gate_used = sem("gate_used")
        c_used = sem("c_used")
        m_ready = sem("m_ready")
        newc_ready = sem("newc_ready")
        out_stored = sem("out_stored")
        acc_done = sem("acc_done")
        acc_added = sem("acc_added")
        s_done = sem("scores_done")
        s_used = sem("scores_used")
        qcur_ready = sem("qcur_ready")
        expd = sem("exp_done")
        pick_ready = sem("pick_ready")
        pickT_done = sem("pickT_done")
        pickT_used = sem("pickT_used")
        iota_ready = sem("iota_ready")
        onehot_ready = sem("onehot_ready")
        onehot_used = sem("onehot_used")
        gt_ready = sem("gt_ready")
        gt_stored = [sem(f"gt_stored{i}") for i in range(2)]
        g_loaded = [sem(f"g_loaded{u}") for u in range(GROUP)]
        gelu_ready = sem("gelu_ready")
        p_mult = sem("p_mult")
        p_ready = sem("p_ready")
        y_ready = sem("y_ready")
        y_stored = [sem(f"y_stored{i}") for i in range(2)]
        fin_loaded = sem("fin_loaded")

        N_W0 = A_MIX
        N_WQ = N_W0 + N_WOUT
        N_U = N_WQ + A_WQ

        block = ctx.enter_context(nc.Block())

        @block.sync
        def _(sp):
            def tile_in(u, src, turn_, first=False):
                if not first:
                    sp.wait_ge(lo_ready, turn_ * GROUP + (u + 1 - GROUP))
                sp.dma_start(raw[:, u, :], src).then_inc(loaded[u], 16)

            def tile_of(t, i):
                return t[ds(i, 1), :, :].rearrange("o p f -> (o p) f")

            sp.dma_start(x[:, :, :], io["x"].rearrange("(t p) d -> p t d", p=P)).then_inc(x_loaded, 16)
            small = [(ident, "ident"), (ones, "ones"), (g1, "norm1_g"), (g2, "norm2_g")]
            for t, n in small:
                sp.dma_start(t[:, :], io[n]).then_inc(consts, 16)
            for u in range(GROUP):
                tile_in(u, io["w_in"][u, :, :], 0, first=True)
            for t, n in ((cos, "cos"), (sin, "sin"), (g16, "g16")):
                sp.dma_start(t[:, :], io[n]).then_inc(ret_consts, 16)
            for t, n in ((dec, "dec"), (dec_s, "dec_s"), (gq, "gq"), (kcol, "kcol")):
                sp.dma_start(t[:, :, :].rearrange("p a b -> p (a b)"), io[n]).then_inc(ret_consts, 16)
            with sp.Fori(1, A_MIX // GROUP) as i:
                for u in range(GROUP):
                    tile_in(u, tile_of(io["w_in"], i * GROUP + u), i)
            for i in range(N_WOUT // GROUP):
                for u in range(GROUP):
                    tile_in(u, io["w_out"][i * GROUP + u, :, :], N_W0 // GROUP + i)
            with sp.Fori(0, A_WQ // GROUP) as i:
                for u in range(GROUP):
                    tile_in(u, tile_of(io["wq"], i * GROUP + u), i + N_WQ // GROUP)
            for g in range(2):
                for u in range(GROUP):
                    tile_in(u, io["u_t"][g * GROUP + u, :, :], N_U // GROUP + g)

            def gates_in(g, u, wait):
                if wait:
                    sp.wait_ge(p_mult, g * GROUP + (u + 1 - GROUP))
                src = gates[:, ds(g * GROUP + u, 1), :].rearrange("p o t -> p (o t)")
                sp.dma_start(gr[:, u, :], src).then_inc(g_loaded[u], 16)

            for i in range(2):
                sp.wait_ge(gt_stored[i], 16 * (T // GT // 2))
            for u in range(GROUP):
                gates_in(0, u, False)
            with sp.Fori(1, NE_GROUPS - 1) as g:
                for u in range(GROUP):
                    gates_in(g, u, True)
                    tile_in(u, tile_of(io["peer_v"], g * GROUP + (u - GROUP)), g * 2 + N_U // GROUP)
                for u in range(GROUP):
                    tile_in(u, tile_of(io["u_t"], g * GROUP + (u + GROUP)), g * 2 + (N_U // GROUP + 1))
            g = NE_GROUPS - 1
            for u in range(GROUP):
                gates_in(g, u, True)
                tile_in(u, io["peer_v"][(g - 1) * GROUP + u, :, :], g * 2 + N_U // GROUP)
            for u in range(GROUP):
                tile_in(u, io["peer_v"][g * GROUP + u, :, :], g * 2 + N_U // GROUP + 1)
            sp.wait_ge(acc_added, 10 * (1 + NE_GROUPS))
            sp.dma_start(fin_g[:, :], io["final_g"]).then_inc(fin_loaded, 16)
            for tt in range(TT):
                sp.wait_ge(y_ready, tt + 1)
                sp.dma_start(io["y"][tt * P:(tt + 1) * P, :], fin_y[:, tt % 2, :]).then_inc(y_stored[tt % 2], 16)
            sp.wait_ge(y_stored[0], 16 * ((TT + 1) // 2))
            sp.wait_ge(y_stored[1], 16 * (TT // 2))

        @block.gpsimd
        def _(pool):
            def low(dst, u, n):
                pool.wait_ge(hi_ready, n + 1)
                hi, lo = dst
                nc.gpsimd.tensor_tensor(lo[u][:, :], raw[:, u, :], hi[u][:, :].bitcast(F32),
                                        ALU.subtract).then_inc(lo_ready, 1)

            A, B = (wa_hi, wa_lo), (wb_hi, wb_lo)
            with pool.Fori(0, A_MIX // GROUP) as i:
                for u in range(GROUP):
                    low(A, u, i * GROUP + u)
            for u in range(GROUP):
                low(B, u, N_W0 + u)
            for u in range(GROUP):
                low(A, u, N_W0 + GROUP + u)
            with pool.Fori(0, A_WQ // GROUP) as i:
                for u in range(GROUP):
                    low(A, u, i * GROUP + (N_WQ + u))
            for u in range(GROUP):
                low(A, u, N_U + u)
            pool.wait_ge(pickT_used, 3 * TT)
            nc.gpsimd.iota(iotaK[:, :, :], [[1, NKEY], [0, BLK]], base=0, channel_multiplier=0,
                           allow_small_or_imprecise_dtypes=True).then_inc(iota_ready, 1)
            for u in range(GROUP):
                low(A, u, N_U + GROUP + u)
            with pool.Fori(1, NE_GROUPS - 1) as g:
                for u in range(GROUP):
                    low(B, u, g * (2 * GROUP) + (N_U + u))
                for u in range(GROUP):
                    low(A, u, g * (2 * GROUP) + (N_U + GROUP + u))
            for u in range(2 * GROUP):
                low(B, u % GROUP, (NE_GROUPS - 1) * 2 * GROUP + N_U + u)

        @block.scalar
        def _(act):
            line = Line(act, act_chain)

            def high_a(u, n, a, ring_free=True):
                act.wait_ge(loaded[u], (n - u) * (16 // GROUP) + 16)
                if ring_free:
                    act.wait_ge(a_used, a - 3)
                nc.scalar.activation(wa_hi[u][:, :], raw[:, u, :], ACT.Copy).then_inc(hi_ready, 1)

            def high_b(u, n):
                act.wait_ge(loaded[u], (n - u) * (16 // GROUP) + 16)
                nc.scalar.activation(wb_hi[u][:, :], raw[:, u, :], ACT.Copy).then_inc(hi_ready, 1)

            def tile_psum(par):
                return ps[:, 2 * par:2 * par + 2, 0:HALF]

            def two(t):
                return t.rearrange("p (a b) -> p a b", a=2)

            def out_of_psum(dst, par, func, a):
                act.wait_ge(a_used, a + 1)
                nc.scalar.activation(two(dst), tile_psum(par), func).then_inc(evac, 1)

            def norm_rows(which):
                for tt in range(TT):
                    line.then(nc.scalar.activation(ps[:, 6:8, :].rearrange("p a b -> p (a b)"), x[:, tt, :],
                                                   ACT.Square, accum_out=ss[:, tt:tt + 1]))
                line.mark(nc.scalar.activation(rms[:, :], ss[:, :], ACT.Sqrt, bias=eps[:, 0:1], scale=1.0 / D))

            act.wait_ge(eps_ready, 1)
            act.wait_ge(x_loaded, 16)
            norm_rows(0)
            high_a(0, 0, 0, False)
            high_a(1, 1, 1, False)

            def head(h, first):
                a0 = h * 8
                for t in range(8):
                    if first and t < 2:
                        high_a(t + 2, t + 2, 0, False)
                    else:
                        high_a((t + 2) % GROUP, a0 + (t + 2), a0 + (t + 2))
                    if t < 4:
                        dst = qk_raw[:, t, :]
                        if t == 0 and first:
                            act.wait_ge(h_ready, 2 * TT)
                        if t == 0 and not first:
                            act.wait_ge(yret_ready, h * 2)
                    elif t < 6:
                        dst = vT[:, t - 4, :]
                    else:
                        dst = yret[:, ds(h * 2 + (t - 6), 1), :].rearrange("p o t -> p (o t)")
                    out_of_psum(dst, t % 2, ACT.Silu if t >= 6 else ACT.Copy, a0 + t)
                for s in range(4):
                    if not first:
                        act.wait_ge(st_ready, h * (1 + STREAMS) + (s - 3))
                    act.dma_start(s_in[:, s, :, :], io["s_in"][ds(h, 1), :, s, :, :].rearrange(
                        "o p a b -> (o p) a b")).then_inc(s_loaded[s], 16)
                for tt in range(TT):
                    act.wait_ge(kvT_done, h * TT + (tt + 1))
                    nc.scalar.activation(kv[:, tt, :], ps[:, 4 + tt % 4, :], ACT.Copy).then_inc(kv_ready, 1)
                for et in range(2):
                    act.wait_ge(o_done, h * 2 + (et + 1))
                    nc.scalar.activation(o_sb[:, et, 0:PROMPT], ps[:, 6 - 2 * et, :], ACT.Copy).then_inc(o_ready, 1)
                for s in range(1 + STREAMS):
                    act.wait_ge(st_ready, h * (1 + STREAMS) + (s + 1))
                    dst = io["sp_out"][ds(h, 1), :, :, :].rearrange("o p a b -> (o p) a b") if s == 0 else \
                        io["ss_out"][ds(h, 1), :, s - 1, :, :].rearrange("o p a b -> (o p) a b")
                    par = s % 2
                    act.dma_start(dst, s_out[:, par, :, :]).then_inc(st_stored[par], 16)
                    if 1 <= s <= 4:
                        act.dma_start(s_in[:, s - 1, :, :], io["s_in"][ds(h, 1), :, s + 3, :, :].rearrange(
                            "o p a b -> (o p) a b")).then_inc(s_loaded[s - 1], 16)
                act.wait_ge(cross_done, h * STREAMS + STREAMS)
                for et in range(2):
                    nc.scalar.activation(o_sb[:, et, PROMPT:T], ps[:, 7 - 2 * et, 0:P], ACT.Copy).then_inc(o_ready, 1)
                for et in range(2):
                    act.wait_ge(o_ready, h * 4 + 4)
                    nc.scalar.activation(o_sb[:, 2 + et, :], o_sb[:, et, :], ACT.Square).then_inc(sq_ready, 1)
                act.wait_ge(ms_done, h + 1)
                nc.scalar.activation(two(o_sb[:, 2, :]), ps[:, 5:8:2, 0:HALF], ACT.Sqrt,
                                     bias=eps[:, 0:1]).then_inc(orms_ready, 1)

            head(0, True)
            with act.Fori(1, HEADS) as h:
                head(h, False)

            def gb_tiles(i, first):
                for u in range(GROUP):
                    a = i * GROUP + (HEADS * 8 + u)
                    high_a((u + 2) % GROUP, a + 2, a + 2)
                    if not (first and u < 2):
                        act.wait_ge(gate_used, i * GROUP + (u - 1))
                    out_of_psum(gate[:, u % 2, :], u % 2, ACT.Sigmoid, a)

            act.wait_ge(yret_ready, 2 * HEADS)
            act.wait_ge(st_stored[0], 80 * HEADS)
            act.wait_ge(st_stored[1], 64 * HEADS)
            act.dma_start(convw[:, :, :].rearrange("p a b -> p (a b)"), io["conv_w"]).then_inc(conv_consts, 16)
            act.dma_start(sconv[:, :, :].rearrange("p a b -> p (a b)"), io["state_conv"]).then_inc(conv_consts, 16)
            gb_tiles(0, True)
            gb_tiles(1, False)

            def conv_tiles(ct, first, last):
                for u in range(GROUP):
                    a = ct * GROUP + (HEADS * 8 + KT + u)
                    if not (last and u >= 2):
                        high_a((u + 2) % GROUP, a + 2, a + 2)
                    if u == 0 and not first:
                        act.wait_ge(c_used, ct)
                    out_of_psum(c_in[:, u, :], u % 2, ACT.Sigmoid if u == 3 else ACT.Copy, a)

            conv_tiles(0, True, False)
            with act.Fori(1, KT - 1) as ct:
                conv_tiles(ct, False, False)
            conv_tiles(KT - 1, False, True)
            act.wait_ge(m_ready, KT)
            act.wait_ge(newc_ready, KT)
            for u in range(GROUP):
                high_b(u, N_W0 + u)
            for u in range(GROUP):
                high_a(u, N_W0 + GROUP + u, A_MIX + u)
            act.dma_start(io["newc"], newc[:, :, :].rearrange("p a b -> p (a b)")).then_inc(out_stored, 16)
            act.wait_ge(out_stored, 16)

            act.wait_ge(acc_added, 10)
            act.dma_start(skT[:, :, :].rearrange("p a b -> p (a b)"), io["skT"]).then_inc(peer_consts, 16)
            act.dma_start(iota16[:, :], io["iota16"]).then_inc(peer_consts, 16)
            norm_rows(1)
            high_a(0, N_WQ, 0, False)
            high_a(1, N_WQ + 1, 0, False)

            def wq_tiles(i, first, last):
                for u in range(GROUP):
                    a = i * GROUP + (A_MIX + u)
                    n = i * GROUP + (N_WQ + u)
                    if not (last and u >= 2):
                        high_a((u + 2) % GROUP, n + 2, a + 2, not (first and u < 2))
                    if first and u == 0:
                        act.wait_ge(h_ready, 4 * TT)
                    dst = qpT[:, ds(i * GROUP + u, 1), :].rearrange("p o t -> p (o t)")
                    out_of_psum(dst, u % 2, ACT.Copy, a)

            wq_tiles(0, True, False)
            with act.Fori(1, A_WQ // GROUP - 1) as i:
                wq_tiles(i, False, False)
            wq_tiles(A_WQ // GROUP - 1, False, True)

            for u in range(GROUP):
                high_a(u, N_U + u, A_MIX + A_WQ + u)

            def retrieval(tt, first):
                if not first:
                    act.wait_ge(s_done, tt)
                act.wait_ge(evac, A_MIX + A_WQ)
                nc.scalar.activation(q_cur[:, :, :], qpT[:, :, ds(tt * P, P)], ACT.Copy).then_inc(qcur_ready, 1)
                act.wait_ge(pick_ready, tt * 2 + 1)
                nc.scalar.activation(pick[:, 2, :], ts[:, :, :].rearrange("p a b -> p (a b)"), ACT.Exp).then_inc(expd, 1)

            retrieval(0, True)
            with act.Fori(1, TT) as tt:
                retrieval(tt, False)

            def gate_blocks(i, half, first):
                for b in range(GT // BLK):
                    if b == 0 and not first:
                        act.wait_ge(gt_stored[half], i * 16)
                    for q in range(2):
                        nb = b * 2 + q
                        act.wait_ge(onehot_used, i * (4 * GT // BLK) + (half * 2 * GT // BLK + nb + 1))
                        src = ps[:, (b % 2) * 2 + q, :].rearrange("p (k t) -> p k t", t=4)
                        dst = gts[half][:, :, b * BLK + q * 4:b * BLK + q * 4 + 4]
                        nc.scalar.activation(dst, src, ACT.Copy).then_inc(gt_ready, 1)
                act.wait_ge(gt_ready, i * (4 * GT // BLK) + (half + 1) * 2 * GT // BLK)
                act.dma_start(gates[:, :, ds(i * (2 * GT) + half * GT, GT)], gts[half][:, :, :]).then_inc(gt_stored[half], 16)

            act.wait_ge(pickT_used, 3 * TT)
            gate_blocks(0, 0, True)
            gate_blocks(0, 1, True)
            with act.Fori(1, T // GT // 2) as i:
                gate_blocks(i, 0, False)
                gate_blocks(i, 1, False)
            for i in range(2):
                act.wait_ge(gt_stored[i], 16 * (T // GT // 2))

            def gelu(g, u, a, wait=True):
                act.wait_ge(a_used, a + 1)
                if wait:
                    act.wait_ge(p_mult, g * GROUP + (u - 1))
                nc.scalar.activation(two(gl[:, u % 2, :]), tile_psum(u % 2), ACT.Gelu).then_inc(evac, 1)

            A_U = A_MIX + A_WQ
            for u in range(GROUP):
                gelu(0, u, A_U + u, u >= 2)
            for u in range(GROUP):
                high_a(u, N_U + GROUP + u, A_U + GROUP + u)
            with act.Fori(1, NE_GROUPS - 1) as g:
                for u in range(GROUP):
                    if u == 0:
                        act.wait_ge(acc_done, g * 10)
                    high_b(u, g * (2 * GROUP) + (N_U + u))
                    gelu(g, u, g * GROUP + (A_U + u))
                for u in range(GROUP):
                    high_a(u, g * (2 * GROUP) + (N_U + GROUP + u), g * GROUP + (A_U + GROUP + u))
            g = NE_GROUPS - 1
            act.wait_ge(acc_done, g * 10)
            for u in range(GROUP):
                high_b(u, g * 2 * GROUP + N_U + u)
                gelu(g, u, g * GROUP + A_U + u)
            act.wait_ge(acc_done, (g + 1) * 10)
            for u in range(GROUP):
                high_b(u, g * 2 * GROUP + N_U + GROUP + u)

            act.wait_ge(acc_added, 10 * (1 + NE_GROUPS))
            norm_rows(2)

        @block.vector
        def _(dve):
            line = Line(dve, dve_chain)

            def then(ins, s, value):
                ins.then_inc(s, 1)
                dve.wait_ge(s, value)

            nc.vector.memset(eps[:, :], EPS).then_inc(eps_ready, 1)

            def newton(r_, t_, mean_, scale, shift):
                line.then(nc.vector.tensor_tensor(t_, r_, r_, ALU.mult))
                if scale is None:
                    line.then(nc.vector.scalar_tensor_tensor(t_, mean_, shift, t_, ALU.add, ALU.mult))
                else:
                    line.then(nc.vector.tensor_scalar(vs[:, :], mean_, scale, shift, ALU.mult, ALU.add))
                    line.then(nc.vector.tensor_tensor(t_, t_, vs[:, :], ALU.mult))
                line.then(nc.vector.tensor_scalar(t_, t_, -0.5, 1.5, ALU.mult, ALU.add))
                line.then(nc.vector.tensor_tensor(r_, r_, t_, ALU.mult))

            def row_factors(which):
                dve.wait_ge(act_chain, (TT + 1) * (which + 1))
                line.then(nc.vector.reciprocal(rstd[:, :], rms[:, :]))
                newton(rstd[:, :], rms[:, :], ss[:, :], 1.0 / D, EPS)

            def norm_to_hT(which, xs_, hf_, gain):
                row_factors(which)
                for tt in range(TT):
                    if tt >= 2:
                        dve.wait_ge(xsT_done, which * 2 * TT + 2 * (tt - 1))
                    nc.vector.tensor_scalar(xs_[:, tt % 2, :], x[:, tt, :], rstd[:, tt:tt + 1], None,
                                            ALU.mult).then_inc(xs_ready, 1)
                    for b in range(2):
                        n = which * 2 * TT + 2 * tt + b
                        dve.wait_ge(xsT_done, n + 1)
                        gb = gain[:, 4 * b:4 * b + 4].unsqueeze(2).broadcast_to([P, 4, P])
                        src = ps[:, 4 + b, :].rearrange("p (k t) -> p k t", k=4)
                        f = hf_[:, b, :].rearrange("p (k t) -> p k t", k=4)
                        hs = (slice(None), slice(4 * b, 4 * b + 4), slice(tt * P, (tt + 1) * P))
                        line.then(nc.vector.tensor_tensor(f, src, gb, ALU.mult))
                        line.then(nc.vector.tensor_copy(h_hi[hs], f))
                        nc.vector.tensor_tensor(h_lo[hs], f, h_hi[hs].bitcast(F32), ALU.subtract).then_inc(h_ready, 1)

            dve.wait_ge(consts, 16 * 4)
            norm_to_hT(0, xs, hf, g1)

            def rotate(h, src, dst, n):
                a, b = qk_raw[:, src, :], qk_raw[:, src + 1, :]
                t = att[:, 0:T]
                line.then(nc.vector.tensor_tensor(dst[:, 0, :], a, cos[:, :], ALU.mult))
                line.then(nc.vector.tensor_tensor(t, b, sin[:, :], ALU.mult))
                line.then(nc.vector.tensor_tensor(dst[:, 0, :], dst[:, 0, :], t, ALU.subtract))
                line.then(nc.vector.tensor_tensor(dst[:, 1, :], a, sin[:, :], ALU.mult))
                line.then(nc.vector.tensor_tensor(t, b, cos[:, :], ALU.mult))
                then(nc.vector.tensor_tensor(dst[:, 1, :], dst[:, 1, :], t, ALU.add), qk_ready, h * 2 + n)

            def head(h, first):
                dve.wait_ge(evac, h * 8 + 2)
                if not first:
                    dve.wait_ge(ms_done, h)
                rotate(h, 0, qT, 1)
                dve.wait_ge(evac, h * 8 + 4)
                rotate(h, 2, kT, 2)

                def row(t, j=None):
                    return t[:, ds(h, 1), :].rearrange("p o t -> p (o t)") if j is None else \
                        t[:, ds(h, 1), j:j + 1].rearrange("p o t -> p (o t)")

                for j in range(PT + 1):
                    dve.wait_ge(att_done, h * 5 + (j + 1))
                    bank, n = [5, 6, 7, 4, 5][j], att_n[j]
                    dd = t_slice(dec, h, n) if j < PT else row(dec_s)
                    then(nc.vector.tensor_tensor(att[:, att_at[j]:att_at[j] + n], ps[:, bank, 0:n], dd, ALU.mult),
                         att_ready, h * 5 + (j + 1))
                for i in range(2):
                    then(nc.vector.tensor_tensor(vT[:, i, 0:P], qT[:, i, PROMPT:T], row(gq), ALU.mult),
                         qg_ready, h * 2 + (i + 1))
                for s in range(PT):
                    then(nc.vector.tensor_scalar(kw[:, s, :], kv[:, s, 0:DK], row(kcol, s), None, ALU.mult),
                         kw_ready, h * 12 + (s + 1))
                dve.wait_ge(st_done, h * 9 + 1)
                if not first:
                    dve.wait_ge(st_stored[0], h * 80)
                then(nc.vector.tensor_copy(s_out[:, 0, :, :].rearrange("p a b -> p (a b)"), ps[:, 6, :]),
                     st_ready, h * 9 + 1)
                for s in range(STREAMS):
                    if s >= 4:
                        dve.wait_ge(st_done, h * 9 + (s - 2))
                    then(nc.vector.tensor_scalar(kw[:, s % 4, :], kv[:, PT, 0:DK], row(kcol, PT + s), None, ALU.mult),
                         kw_ready, h * 12 + (PT + s + 1))
                    dve.wait_ge(st_done, h * 9 + (s + 2))
                    par = (s + 1) % 2
                    if par == 0:
                        dve.wait_ge(st_stored[0], h * 80 + 16 * ((s + 1) // 2))
                    elif s >= 2:
                        dve.wait_ge(st_stored[1], h * 64 + 16 * (s // 2))
                    elif not first:
                        dve.wait_ge(st_stored[1], h * 64)
                    bank = [6, 4][(s + 1) % 2]
                    dve.wait_ge(cross_done, h * STREAMS + (s + 1))
                    then(nc.vector.scalar_tensor_tensor(
                        s_out[:, par, :, :].rearrange("p a b -> p (a b)"),
                        s_in[:, s % 4, :, :].rearrange("p a b -> p (a b)"),
                        g16[:, ds(h, 1)], ps[:, bank, :], ALU.mult, ALU.add), st_ready, h * 9 + (s + 2))
                dve.wait_ge(orms_ready, h + 1)
                line.then(nc.vector.reciprocal(o_sb[:, 3, :], o_sb[:, 2, :]))
                newton(o_sb[:, 3, :].rearrange("p (a b) -> p a b", a=2), o_sb[:, 2, :].rearrange("p (a b) -> p a b", a=2),
                       ps[:, 5:8:2, 0:HALF], None, EPS)
                for et in range(2):
                    yr = yret[:, ds(h * 2 + et, 1), :].rearrange("p o t -> p (o t)")
                    line.then(nc.vector.tensor_tensor(o_sb[:, et, :], o_sb[:, et, :], o_sb[:, 3, :], ALU.mult))
                    then(nc.vector.tensor_tensor(yr, yr, o_sb[:, et, :], ALU.mult), yret_ready, h * 2 + (et + 1))

            def t_slice(t, h, n):
                return t[:, ds(h, 1), 0:n].rearrange("p o t -> p (o t)")

            dve.wait_ge(ret_consts, 16 * 7)
            R_PER = 2 * 5 + 1 + 4 + 2
            line.turn(0, R_PER)
            head(0, True)
            line.close(1)
            with dve.Fori(1, HEADS) as h:
                line.turn(h - 1, R_PER)
                head(h, False)
            line.close(HEADS - 1)

            for n in range(KT):
                dve.wait_ge(evac, HEADS * 8 + n + 1)
                nc.vector.tensor_tensor(yret[:, n, :], yret[:, n, :], gate[:, n % 2, :], ALU.mult).then_inc(gate_used, 1)

            dve.wait_ge(conv_consts, 16 * 2)
            dve.wait_ge(gate_used, KT)
            line.then(nc.vector.memset(ub[:, 0:2], 0.0))
            uv = ub[:, 2 + PROMPT:UB].rearrange("p (b s) -> p b s", b=STREAMS)
            C_PER = 2 + 1 + 3 + 1 + 3 + 1

            cvs = cv[:, 2 + PROMPT:UB].rearrange("p (b s) -> p b s", b=STREAMS)[:, :, 0:STEP]

            def streams_of(t):
                return t.rearrange("p (b s) -> p b s", b=STREAMS)

            with dve.Fori(0, KT) as ct:
                line.turn(ct, C_PER)
                cc, ch, cb, ga = (c_in[:, i, :] for i in range(4))
                dve.wait_ge(evac, ct * 4 + (HEADS * 8 + KT + 2))
                line.then(nc.vector.tensor_tensor(ub[:, 2:2 + PROMPT], cc[:, 0:PROMPT], ch[:, 0:PROMPT], ALU.mult))
                line.then(nc.vector.tensor_tensor(uv[:, :, 2:], streams_of(cc[:, PROMPT:T]), streams_of(ch[:, PROMPT:T]), ALU.mult))
                line.then(nc.vector.tensor_copy(uv[:, :, 0:2], sconv[:, ds(ct, 1), :].rearrange("p o (b s) -> p (o b) s", b=STREAMS)))
                w = [convw[:, ds(ct, 1), i:i + 1].rearrange("p o t -> p (o t)") for i in range(CONV_W)]
                line.then(nc.vector.tensor_scalar(cv[:, 0:CW], ub[:, 0:CW], w[0], None, ALU.mult))
                line.then(nc.vector.scalar_tensor_tensor(cv[:, 0:CW], ub[:, 1:1 + CW], w[1], cv[:, 0:CW], ALU.mult, ALU.add))
                line.then(nc.vector.scalar_tensor_tensor(cv[:, 0:CW], ub[:, 2:2 + CW], w[2], cv[:, 0:CW], ALU.mult, ALU.add))
                nr = newc[:, ds(ct, 1), :].rearrange("p o t -> p (o t)")
                line.then(nc.vector.tensor_copy(nr[:, 0:2], ub[:, PROMPT:PROMPT + 2]))
                nc.vector.tensor_copy(nr[:, 2:].rearrange("p (b s) -> p b s", b=STREAMS), uv[:, :, STEP:]).then_inc(newc_ready, 1)
                dve.wait_ge(newc_ready, ct + 1)
                dve.wait_ge(evac, ct * 4 + (HEADS * 8 + KT + 4))
                line.then(nc.vector.tensor_tensor(y[:, 0:PROMPT], cv[:, 0:PROMPT], cb[:, 0:PROMPT], ALU.mult))
                line.then(nc.vector.tensor_tensor(streams_of(y[:, PROMPT:T]), cvs, streams_of(cb[:, PROMPT:T]), ALU.mult))
                line.then(nc.vector.tensor_tensor(y[:, :], y[:, :], ga, ALU.mult))
                nc.vector.tensor_tensor(y[:, :], y[:, :], yret[:, ds(ct, 1), :].rearrange("p o t -> p (o t)"), ALU.add).then_inc(c_used, 1)
                dve.wait_ge(c_used, ct + 1)
                mh = m_hi[:, ds(ct, 1), :].rearrange("p o t -> p (o t)")
                ml = m_lo[:, ds(ct, 1), :].rearrange("p o t -> p (o t)")
                line.then(nc.vector.tensor_copy(mh, y[:, :]))
                nc.vector.tensor_tensor(ml, y[:, :], mh.bitcast(F32), ALU.subtract).then_inc(m_ready, 1)
                dve.wait_ge(m_ready, ct + 1)
            line.close(KT)

            def add_products(stage):
                for n in range(10):
                    tt, dh = n // 2, n % 2
                    dve.wait_ge(acc_done, stage * 10 + (n + 1))
                    sl = x[:, tt, dh * 512:(dh + 1) * 512]
                    nc.vector.tensor_tensor(sl, sl, ps[:, 4 + n % 2, :], ALU.add).then_inc(acc_added, 1)

            add_products(0)
            norm_to_hT(1, xs2, hf2, g2)

            dve.wait_ge(peer_consts, 16 * 2)
            dve.wait_ge(h_ready, 4 * TT)
            K_PER = 8 + 1 + 8 + 1 + 3 + 6 + 2 + 1 + 3

            def settle():
                line.mark(nc.vector.memset(nothing[:, 0:1], 0.0))

            def top_sixteen(rows, less, values, places):
                every = list(enumerate(zip(rows, less)))
                settle()
                for s, (row, _) in every:
                    last = nc.vector.max(values[:, s, 0:8], row)
                line.then(last)
                settle()
                for s, (row, low) in every:
                    last = nc.vector.match_replace(low, values[:, s, 0:8], row, LOWEST)
                line.then(last)
                settle()
                for s, (row, low) in every:
                    nc.vector.max(values[:, s, 8:16], low)
                    last = nc.vector.max_index(places[:, s, 0:8], values[:, s, 0:8], row)
                line.then(last)
                settle()
                for s, (_, low) in every:
                    last = nc.vector.max_index(places[:, s, 8:16], values[:, s, 8:16], low)
                line.then(last)

            def retrieval(tt, first):
                dve.wait_ge(s_done, tt + 1)
                if not first:
                    dve.wait_ge(pickT_used, tt * 3)
                sc = [ps[:, s // 4, (s % 4) * NKEY:(s % 4 + 1) * NKEY] for s in range(SIDES)]
                top_sixteen(sc, [rest[:, s, :] for s in range(SIDES)], val, idx)
                nc.vector.tensor_copy(idx_f[:, :, :], idx[:, :, :]).then_inc(s_used, 1)
                dve.wait_ge(s_used, tt + 1)
                vv = val[:, :, :].rearrange("p (h s) k -> p h s k", s=2)
                c4 = cand[:, :, :].rearrange("p h (i j) -> p h i j", i=TOPK)
                line.then(nc.vector.tensor_tensor(
                    c4, vv[:, :, 0, :].unsqueeze(3).broadcast_to([P, PH, TOPK, TOPK]),
                    vv[:, :, 1, :].unsqueeze(2).broadcast_to([P, PH, TOPK, TOPK]), ALU.add))
                top_sixteen([cand[:, h, :] for h in range(PH)], [cand2[:, h, :] for h in range(PH)], ts, tp)
                line.then(nc.vector.tensor_copy(mx[:, 0, :], ts[:, :, 0]))
                nc.vector.tensor_tensor(ts[:, :, :], ts[:, :, :], mx[:, 0, :].unsqueeze(2).broadcast_to([P, PH, TOPK]),
                                        ALU.subtract).then_inc(pick_ready, 1)
                tpf = tp[:, :, :].rearrange("p h k -> p (h k)")
                line.then(nc.vector.tensor_scalar(tij[:, 0, :], tpf, 4, None, ALU.logical_shift_right))
                line.then(nc.vector.tensor_scalar(tij[:, 1, :], tpf, 15, None, ALU.bitwise_and))
                line.then(nc.vector.tensor_copy(tij_f[:, :, :], tij[:, :, :]))
                ix = idx_f[:, :, :].rearrange("p (h s) k -> p h s k", s=2)
                for side in range(2):
                    eq = cand[:, :, :].rearrange("p h (k i) -> p (h k) i", i=TOPK)
                    line.then(nc.vector.tensor_tensor(
                        eq, tij_f[:, side, :].unsqueeze(2).broadcast_to([P, PH * TOPK, TOPK]),
                        iota16[:, :].unsqueeze(1).broadcast_to([P, PH * TOPK, TOPK]), ALU.is_equal))
                    eq4 = cand[:, :, :].rearrange("p h (k i) -> p h k i", i=TOPK)
                    line.then(nc.vector.tensor_tensor(
                        eq4, eq4, ix[:, :, side, :].unsqueeze(2).broadcast_to([P, PH, TOPK, TOPK]), ALU.mult))
                    if side == 0:
                        line.then(nc.vector.tensor_reduce(pick[:, 0, :], eq, AX.X, ALU.add))
                    else:
                        line.then(nc.vector.tensor_reduce(pick[:, 1, :], eq, AX.X, ALU.add))
                dve.wait_ge(expd, tt + 1)
                ex = pick[:, 2, :].rearrange("p (h k) -> p h k", h=PH)
                line.then(nc.vector.tensor_reduce(mx[:, 1, :], ex, AX.X, ALU.add))
                line.then(nc.vector.reciprocal(mx[:, 2, :], mx[:, 1, :]))
                nc.vector.tensor_tensor(ex, ex, mx[:, 2, :].unsqueeze(2).broadcast_to([P, PH, TOPK]),
                                        ALU.mult).then_inc(pick_ready, 1)
                tok = ds(tt * P, P)
                dve.wait_ge(pickT_done, tt + 1)
                nc.vector.tensor_copy(k1T[:, tok], ps[:, 4, 0:P]).then_inc(pickT_used, 1)
                nc.vector.tensor_copy(k2T[:, tok], ps[:, 4, P:2 * P]).then_inc(pickT_used, 1)
                line.then(nc.vector.tensor_copy(w3T[:, 0, tok], ps[:, 4, 2 * P:3 * P]))
                nc.vector.tensor_tensor(wT[:, :], ps[:, 4, 2 * P:3 * P], w3T[:, 0, tok], ALU.subtract).then_inc(pickT_used, 1)
                dve.wait_ge(pickT_used, tt * 3 + 3)
                line.then(nc.vector.tensor_copy(w3T[:, 1, tok], wT[:, :]))
                line.then(nc.vector.tensor_tensor(wT2[:, :], wT[:, :], w3T[:, 1, tok], ALU.subtract))
                line.then(nc.vector.tensor_copy(w3T[:, 2, tok], wT2[:, :]))
            line.turn(0, K_PER)
            retrieval(0, True)
            line.close(1)
            with dve.Fori(1, TT) as tt:
                line.turn(tt - 1, K_PER)
                retrieval(tt, False)
            line.close(TT - 1)

            dve.wait_ge(iota_ready, 1)

            def onehots(i, par, first):
                if not first:
                    dve.wait_ge(onehot_used, i * 4 + (2 * par - 2))
                tok = ds((i * 2 + par) * BLK, BLK)

                def rows(t):
                    return t.unsqueeze(1).broadcast_to([P, NKEY, BLK])

                line.then(nc.vector.tensor_tensor(eq1[:, par, :, :], iotaK[:, :, :], rows(k1T[:, tok]), ALU.is_equal))
                line.then(nc.vector.tensor_tensor(eq2[:, par, :, :], iotaK[:, :, :], rows(k2T[:, tok]), ALU.is_equal))
                for q in range(3):
                    nc.vector.tensor_tensor(ew[:, par, q, :, :], eq1[:, par, :, :], rows(w3T[:, q, tok]),
                                            ALU.mult).then_inc(onehot_ready, 1)

            for par in range(2):
                onehots(0, par, True)
            with dve.Fori(1, T // BLK // 2) as i:
                line.turn(i - 1, 4)
                for par in range(2):
                    onehots(i, par, False)
            line.close(T // BLK // 2 - 1)

            def weigh(g, u, par, wait_p):
                dve.wait_ge(evac, g * GROUP + (A_MIX + A_WQ + u + 1))
                dve.wait_ge(g_loaded[u], g * 16 + 16)
                then(nc.vector.tensor_tensor(p32[:, :], gl[:, u % 2, :], gr[:, u, :], ALU.mult), p_mult, g * GROUP + (u + 1))
                if wait_p is not None:
                    dve.wait_ge(acc_done, wait_p)
                line.then(nc.vector.tensor_copy(p_hi[par][:, u, :], p32[:, :]))
                nc.vector.tensor_tensor(p_lo[par][:, u, :], p32[:, :], p_hi[par][:, u, :].bitcast(F32),
                                        ALU.subtract).then_inc(p_ready, 1)
                dve.wait_ge(p_ready, g * GROUP + (u + 1))

            for u in range(GROUP):
                weigh(0, u, 0, None)
            for u in range(GROUP):
                weigh(1, u, 1, None)
            add_products(1)
            with dve.Fori(0, NE_GROUPS // 2 - 1) as i:
                line.turn(i, 2 * GROUP)
                for par in range(2):
                    g = i * 2 + (2 + par)
                    for u in range(GROUP):
                        weigh(g, u, par, g * 10 if u == 0 else None)
                    add_products(g)
            line.close(NE_GROUPS // 2 - 1)
            add_products(NE_GROUPS)

            row_factors(2)
            dve.wait_ge(fin_loaded, 16)
            for tt in range(TT):
                if tt >= 2:
                    dve.wait_ge(y_stored[tt % 2], 16 * (tt // 2))
                nc.vector.scalar_tensor_tensor(fin_y[:, tt % 2, :], x[:, tt, :], rstd[:, tt:tt + 1], fin_g[:, :],
                                               ALU.mult, ALU.mult).then_inc(y_ready, 1)

        @block.tensor
        def _(pe):
            def product(u, par, n, a, wait_evac=True):
                pe.wait_ge(lo_ready, n + 1)
                if wait_evac:
                    pe.wait_ge(evac, a - 1)
                for hv in range(2):
                    out = ps[:, 2 * par + hv, 0:HALF]
                    tok = slice(hv * HALF, (hv + 1) * HALF)
                    for k in range(KT):
                        cols = slice(k * P, (k + 1) * P)
                        nc.tensor.matmul(out, wa_hi[u][:, cols], h_hi[:, k, tok], start=(k == 0), stop=False)
                        nc.tensor.matmul(out, wa_hi[u][:, cols], h_lo[:, k, tok], start=False, stop=False)
                        last = nc.tensor.matmul(out, wa_lo[u][:, cols], h_hi[:, k, tok], start=False, stop=(k == KT - 1))
                last.then_inc(a_used, 1)

            def by_token(lhs, rhs, stage, first=False, done=None):
                for n in range(10):
                    tt, dh = n // 2, n % 2
                    if not (first and n < 2):
                        pe.wait_ge(acc_added, stage * 10 + (n - 1))
                    out = ps[:, 4 + n % 2, :]
                    tok = slice(tt * P, (tt + 1) * P)
                    cols = slice(dh * 512, (dh + 1) * 512)
                    for i, ((lh, ll), (rh, rl)) in enumerate(zip(lhs, rhs)):
                        e_ = i == len(lhs) - 1
                        nc.tensor.matmul(out, lh[:, tok], rh[:, cols], start=(i == 0), stop=False)
                        nc.tensor.matmul(out, ll[:, tok], rh[:, cols], start=False, stop=False)
                        last = nc.tensor.matmul(out, lh[:, tok], rl[:, cols], start=False, stop=e_)
                    last.then_inc(acc_done, 1)

            def norm_transposes(which, xs_):
                for tt in range(TT):
                    pe.wait_ge(xs_ready, which * TT + tt + 1)
                    for b in range(2):
                        if tt:
                            pe.wait_ge(h_ready, which * 2 * TT + 2 * (tt - 1) + b + 1)
                        for k in range(4):
                            cols = slice((4 * b + k) * P, (4 * b + k + 1) * P)
                            last = nc.tensor.transpose(ps[:, 4 + b, k * P:(k + 1) * P], xs_[:, tt % 2, cols], ident[:, :])
                        last.then_inc(xsT_done, 1)

            pe.wait_ge(consts, 16 * 4)
            norm_transposes(0, xs)
            pe.wait_ge(h_ready, 2 * TT)

            def head(h, first):
                for t in range(8):
                    product(t % GROUP, t % 2, h * 8 + t, h * 8 + t, not (first and t < 2))
                pe.wait_ge(qk_ready, h * 2 + 2)
                pe.wait_ge(evac, h * 8 + 6)
                for tt in range(TT):
                    if tt == 4:
                        pe.wait_ge(kv_ready, h * TT + 1)
                    elif not first:
                        pe.wait_ge(yret_ready, h * 2)
                    for i, src in enumerate((kT[:, 0, :], kT[:, 1, :], vT[:, 0, :], vT[:, 1, :])):
                        last = nc.tensor.transpose(ps[:, 4 + tt % 4, i * P:(i + 1) * P], src[:, tt * P:(tt + 1) * P], ident[:, :])
                    last.then_inc(kvT_done, 1)
                for j in range(PT + 1):
                    n, bank = att_n[j], [5, 6, 7, 4, 5][j]
                    q0 = j * P
                    if j < PT:
                        pe.wait_ge(kv_ready, h * TT + (j + 2))
                    else:
                        pe.wait_ge(att_ready, h * 5 + 1)
                    for d in range(2):
                        last = nc.tensor.matmul(ps[:, bank, 0:n], kT[:, d, q0:q0 + P], qT[:, d, q0:q0 + n],
                                                start=(d == 0), stop=(d == 1))
                    last.then_inc(att_done, 1)
                pe.wait_ge(att_ready, h * 5 + 5)
                for et in range(2):
                    cols = slice(DK + et * P, DK + (et + 1) * P)
                    for j in range(PT):
                        last = nc.tensor.matmul(ps[:, 6 - 2 * et, j * P:PROMPT], kv[:, j, cols],
                                                att[:, att_at[j]:att_at[j] + att_n[j]], start=(j == 0), stop=(j == PT - 1))
                    last.then_inc(o_done, 1)
                pe.wait_ge(o_ready, h * 4 + 1)
                pe.wait_ge(kw_ready, h * 12 + PT)
                for d in range(2):
                    for j in range(PT):
                        last = nc.tensor.matmul(ps[:, 6, d * DV:(d + 1) * DV], kw[:, j, d * P:(d + 1) * P],
                                                kv[:, j, DK:DK + DV], start=(j == 0), stop=(j == PT - 1))
                last.then_inc(st_done, 1)
                for et in range(2):
                    cols = slice(DK + et * P, DK + (et + 1) * P)
                    nc.tensor.matmul(ps[:, 7 - 2 * et, 0:P], kv[:, PT, cols], att[:, att_at[4]:att_at[4] + P],
                                     start=True, stop=False)
                pe.wait_ge(qg_ready, h * 2 + 2)
                pe.wait_ge(o_ready, h * 4 + 2)
                for s in range(STREAMS):
                    pe.wait_ge(s_loaded[s % 4], h * 32 + 16 * (s // 4 + 1))
                    for et in range(2):
                        for d in range(2):
                            last = nc.tensor.matmul(
                                ps[:, 7 - 2 * et, s * STEP:(s + 1) * STEP], s_in[:, s % 4, d, et * P:(et + 1) * P],
                                vT[:, d, s * STEP:(s + 1) * STEP], start=False, stop=(s == STREAMS - 1 and d == 1))
                    last.then_inc(cross_done, 1)
                    pe.wait_ge(kw_ready, h * 12 + (PT + s + 1))
                    if s >= 1:
                        pe.wait_ge(st_ready, h * 9 + s)
                    bank = [6, 4][(s + 1) % 2]
                    for d in range(2):
                        last = nc.tensor.matmul(ps[:, bank, d * DV:(d + 1) * DV], kw[:, s % 4, d * P:(d + 1) * P],
                                                kv[:, PT, DK:DK + DV], start=True, stop=True)
                    last.then_inc(st_done, 1)

            def mean_squares(h):
                pe.wait_ge(sq_ready, h * 2 + 2)
                for hv in range(2):
                    for et in range(2):
                        last = nc.tensor.matmul(ps[:, 5 + 2 * hv, 0:HALF], ones[:, :],
                                                o_sb[:, 2 + et, hv * HALF:(hv + 1) * HALF], start=(et == 0), stop=(et == 1))
                last.then_inc(ms_done, 1)

            head(0, True)
            mean_squares(0)
            with pe.Fori(1, HEADS) as h:
                head(h, False)
                mean_squares(h)

            with pe.Fori(HEADS * 8 // GROUP, A_MIX // GROUP) as i:
                for u in range(GROUP):
                    product(u, u % 2, i * GROUP + u, i * GROUP + u)

            pe.wait_ge(m_ready, KT)
            pe.wait_ge(lo_ready, N_W0 + N_WOUT)
            by_token([(m_hi[:, kk, :], m_lo[:, kk, :]) for kk in range(KT)],
                     [(wb_hi[u][:, :], wb_lo[u][:, :]) for u in range(GROUP)]
                     + [(wa_hi[u][:, :], wa_lo[u][:, :]) for u in range(GROUP)], 0, first=True)

            norm_transposes(1, xs2)
            pe.wait_ge(h_ready, 4 * TT)
            with pe.Fori(0, A_WQ // GROUP) as i:
                for u in range(GROUP):
                    product(u, u % 2, i * GROUP + (N_WQ + u), i * GROUP + (A_MIX + u))

            pe.wait_ge(peer_consts, 16 * 2)
            pe.wait_ge(evac, A_MIX + A_WQ)

            def retrieval(tt, first):
                pe.wait_ge(qcur_ready, tt + 1)
                if not first:
                    pe.wait_ge(s_used, tt)
                for s in range(SIDES):
                    last = nc.tensor.matmul(ps[:, s // 4, (s % 4) * NKEY:(s % 4 + 1) * NKEY], q_cur[:, s, :],
                                            skT[:, s % 2, :], start=True, stop=True)
                last.then_inc(s_done, 1)
                pe.wait_ge(pick_ready, tt * 2 + 2)
                for i in range(3):
                    last = nc.tensor.transpose(ps[:, 4, i * P:(i + 1) * P], pick[:, i, :], ident[:, :])
                last.then_inc(pickT_done, 1)

            retrieval(0, True)
            with pe.Fori(1, TT) as tt:
                retrieval(tt, False)

            pe.wait_ge(s_used, TT)

            def gate_block(i, par, first):
                pe.wait_ge(onehot_ready, i * 6 + (3 * par + 3))
                for q in range(2):
                    if not first:
                        pe.wait_ge(gt_ready, i * 4 + (2 * par + q - 3))
                    bank = ps[:, 2 * par + q, :].rearrange("p (k t) -> p k t", t=4)
                    for t in range(4):
                        b = q * 4 + t
                        for part in range(3):
                            last = nc.tensor.matmul(bank[:, :, t], eq2[:, par, :, b], ew[:, par, part, :, b],
                                                    start=(part == 0), stop=(part == 2))
                    last.then_inc(onehot_used, 1)

            for par in range(2):
                gate_block(0, par, True)
            with pe.Fori(1, T // BLK // 2) as i:
                for par in range(2):
                    gate_block(i, par, False)
            pe.wait_ge(gt_ready, 2 * T // BLK)

            A_U = A_MIX + A_WQ

            def down(g, par, n):
                pe.wait_ge(lo_ready, n + 1)
                pe.wait_ge(p_ready, g * GROUP + GROUP)
                by_token([(p_hi[par][:, u, :], p_lo[par][:, u, :]) for u in range(GROUP)],
                         [(wb_hi[u][:, :], wb_lo[u][:, :]) for u in range(GROUP)], g + 1)

            def up(g):
                for u in range(GROUP):
                    product(u, u % 2, g * (2 * GROUP) + (N_U - GROUP + u), g * GROUP + (A_U + u))

            for u in range(GROUP):
                product(u, u % 2, N_U + u, A_U + u)
            with pe.Fori(0, NE_GROUPS // 2 - 1) as i:
                for par in range(2):
                    g = i * 2 + (1 + par)
                    up(g)
                    down(g - 1, par, g * (2 * GROUP) + (N_U + GROUP - 1))
            g = NE_GROUPS - 1
            up(g)
            down(g - 1, 0, g * 2 * GROUP + N_U + GROUP - 1)
            down(g, 1, g * 2 * GROUP + N_U + 2 * GROUP - 1)



OUTS = {
    "y": (T, D), "newc": (P, KT * (2 + 2 * STREAMS)),
    "sp_out": (HEADS, P, 2, DV), "ss_out": (HEADS, P, STREAMS, 2, DV),
}


def kernel(x_prompt, x_sample, state_conv, state_ret, norm1_g, w_in, conv_w, w_out, norm2_g,
           peer_wq, peer_subkeys, peer_u, peer_v, final_g):
    import concourse.bacc as bacc
    from concourse.bass_utils import run_bass_kernel_spmd

    def column_tiles(w):
        w = np.asarray(w).reshape(KT, P, -1, P)
        return w.transpose(2, 1, 0, 3).reshape(w.shape[2], P, D)

    x = np.concatenate([np.asarray(x_prompt).reshape(-1, D), np.asarray(x_sample).reshape(-1, D)])
    arrays = {
        "x": x,
        "w_in": column_tiles(w_in[0])[w_in_order()],
        "w_out": np.asarray(w_out[0]).reshape(KT, P, D),
        "wq": column_tiles(peer_wq[0]),
        "u_t": np.asarray(peer_u[0]).reshape(NKEY, P, KT, P).transpose(0, 3, 2, 1).reshape(NKEY, P, D),
        "peer_v": np.asarray(peer_v[0]).reshape(NKEY, P, D),
        "norm1_g": np.asarray(norm1_g[0]).reshape(KT, P).T,
        "norm2_g": np.asarray(norm2_g[0]).reshape(KT, P).T,
        "final_g": np.broadcast_to(np.asarray(final_g)[None, :], (P, D)),
        "conv_w": np.asarray(conv_w[0]).reshape(CONV_W, KT, P).transpose(2, 1, 0).reshape(P, -1),
        "state_conv": np.asarray(state_conv[0]).reshape(STREAMS * 2, KT, P).transpose(2, 1, 0).reshape(P, -1),
        "s_in": np.asarray(state_ret[0]).reshape(STREAMS, HEADS, 2, P, DV).transpose(1, 3, 0, 2, 4),
        "skT": np.asarray(peer_subkeys[0]).transpose(2, 0, 1).reshape(P, -1),
    }
    arrays.update(tables())
    arrays = {k: np.ascontiguousarray(v) for k, v in arrays.items()}

    nc = bacc.Bacc("TRN2", target_bir_lowering=False, num_devices=1)
    io, named = {}, {}
    for name, a in arrays.items():
        named["in_" + name] = a
        io[name] = nc.dram_tensor("in_" + name, a.shape, mybir.dt.from_np(a.dtype), kind="ExternalInput").ap()
    for name, shape in OUTS.items():
        io[name] = nc.dram_tensor("out_" + name, shape, F32, kind="ExternalOutput").ap()
    build_program(nc, io)
    got = run_bass_kernel_spmd(nc, [named], core_ids=[0]).results[0]

    y = got["out_y"]
    newc = got["out_newc"].reshape(P, KT, 2 + 2 * STREAMS).transpose(2, 1, 0).reshape(2 + 2 * STREAMS, D)
    sp = got["out_sp_out"].transpose(0, 2, 1, 3).reshape(1, 1, HEADS, DK, DV)
    st = got["out_ss_out"].transpose(2, 0, 3, 1, 4).reshape(1, STREAMS, HEADS, DK, DV)
    return (y[:PROMPT].reshape(1, PROMPT, D), y[PROMPT:].reshape(STREAMS, STEP, D),
            newc[:2].reshape(1, 1, 2, D), sp, newc[2:].reshape(1, STREAMS, 2, D), st)
```
